# Optimizing a Trainium2 kernel written in Bass

```python
import jax, jax.numpy as jnp
from jax import lax
import numpy as np

D_MODEL = 1024
BATCH = 1
SEQ = 1024
DEPTH = 1

MIX_WIDTH = D_MODEL
POOL_WINDOWS = (2, 4, 8, 16)
N_POOL_GROUPS = 4
POOL_WIDTH = D_MODEL // 4
POOL_GROUP = POOL_WIDTH // N_POOL_GROUPS
CONV_WIDTH = D_MODEL // 4
CONV_HEADS = 4
CONV_K = 3
HEAD_DIM = 64
N_Q_HEADS = (D_MODEL // 2) // HEAD_DIM
N_KV_HEADS = 2
GQA_GROUP = N_Q_HEADS // N_KV_HEADS
Q_WIDTH = N_Q_HEADS * HEAD_DIM
KV_WIDTH = N_KV_HEADS * HEAD_DIM
WINDOW = 128
BLOCK = 128
IN_SIZES = (POOL_WIDTH, CONV_WIDTH, CONV_WIDTH, CONV_WIDTH, Q_WIDTH, KV_WIDTH, KV_WIDTH)
IN_WIDTH = POOL_WIDTH + 3 * CONV_WIDTH + Q_WIDTH + 2 * KV_WIDTH
D_FF = 2816
EPS = 1e-6
NEG_INF = -1e30

kernel_name = "hybrid_pool_conv_swa_sink_block"

def rms_norm(x, g):
    xf = x.astype(jnp.float32)
    y = xf * lax.rsqrt(jnp.mean(xf * xf, axis=-1, keepdims=True) + EPS)
    return (y * g.astype(jnp.float32)).astype(x.dtype)

def causal_dwconv(u, w):
    k = w.shape[0]
    s = u.shape[1]
    up = jnp.pad(u, ((0, 0), (k - 1, 0), (0, 0)))
    y = up[:, 0:s, :] * w[0]
    for j in range(1, k):
        y = y + up[:, j:j + s, :] * w[j]
    return y

def pool_mixer(u, w_grp, scale):
    bn, s, _ = u.shape
    uf = u.astype(jnp.float32)
    cs = jnp.pad(jnp.cumsum(uf, axis=1), ((0, 0), (1, 0), (0, 0)))
    cnt_base = jnp.arange(1, s + 1, dtype=jnp.int32)
    outs = []
    for g, w in enumerate(POOL_WINDOWS):
        c = cs[:, :, g * POOL_GROUP:(g + 1) * POOL_GROUP]
        lagged = jnp.pad(c, ((0, 0), (w - 1, 0), (0, 0)))[:, :s, :]
        cnt = jnp.minimum(cnt_base, w).astype(jnp.float32)
        mean = (c[:, 1:, :] - lagged) / cnt[None, :, None]
        outs.append(mean - uf[:, :, g * POOL_GROUP:(g + 1) * POOL_GROUP])
    d = jnp.stack(outs, axis=2)
    y = jnp.einsum('bsgc,gcd->bsgd', d, w_grp.astype(jnp.float32)).reshape(bn, s, POOL_WIDTH)
    return (y * scale.astype(jnp.float32)).astype(u.dtype)

def swa_sink_attention(q, k, v, sinks):
    bn, s, _ = q.shape
    nb = s // BLOCK
    qb = q.reshape(bn, nb, BLOCK, N_KV_HEADS, GQA_GROUP, HEAD_DIM)
    kb = k.reshape(bn, nb, BLOCK, N_KV_HEADS, HEAD_DIM)
    vb = v.reshape(bn, nb, BLOCK, N_KV_HEADS, HEAD_DIM)
    pad = ((0, 0), (1, 0), (0, 0), (0, 0), (0, 0))
    kk = jnp.concatenate([jnp.pad(kb, pad)[:, :nb], kb], axis=2)
    vv = jnp.concatenate([jnp.pad(vb, pad)[:, :nb], vb], axis=2)
    scores = jnp.einsum('bnqhgd,bnkhd->bnhgqk', qb, kk,
                        preferred_element_type=jnp.float32) * (HEAD_DIM ** -0.5)
    blk = jnp.arange(nb, dtype=jnp.int32)[:, None, None] * BLOCK
    qpos = blk + jnp.arange(BLOCK, dtype=jnp.int32)[None, :, None]
    kpos = blk - BLOCK + jnp.arange(2 * BLOCK, dtype=jnp.int32)[None, None, :]
    diff = qpos - kpos
    mask = (diff >= 0) & (diff < WINDOW) & (kpos >= 0)
    scores = jnp.where(mask[None, :, None, None, :, :], scores, NEG_INF)
    sink = jnp.broadcast_to(
        sinks.astype(jnp.float32).reshape(1, 1, N_KV_HEADS, GQA_GROUP, 1, 1),
        scores.shape[:-1] + (1,))
    probs = jax.nn.softmax(jnp.concatenate([scores, sink], axis=-1), axis=-1)[..., :2 * BLOCK]
    out = jnp.einsum('bnhgqk,bnkhd->bnqhgd', probs.astype(vv.dtype), vv)
    return out.reshape(bn, s, Q_WIDTH)

def setup_inputs(seed: int = 0) -> dict:
    key = jax.random.key(seed)
    ks = jax.random.split(key, 16)
    f32 = jnp.float32

    def nrm(k, shape, scale):
        return jax.random.normal(k, shape, f32) * scale

    def gain(k, width):
        return 1.0 + 0.1 * jax.random.normal(k, (DEPTH, width), f32)

    return {
        "x": nrm(ks[0], (BATCH, SEQ, D_MODEL), 1.0),
        "norm_mix_pre": gain(ks[1], D_MODEL),
        "w_in": nrm(ks[2], (DEPTH, D_MODEL, IN_WIDTH), D_MODEL ** -0.5),
        "pool_w": nrm(ks[3], (DEPTH, N_POOL_GROUPS, POOL_GROUP, POOL_GROUP), POOL_GROUP ** -0.5),
        "pool_scale": gain(ks[4], POOL_WIDTH),
        "conv_w": nrm(ks[5], (DEPTH, CONV_K, CONV_WIDTH), CONV_K ** -0.5),
        "attn_sinks": nrm(ks[6], (DEPTH, N_Q_HEADS), 0.5),
        "w_o": nrm(ks[7], (DEPTH, MIX_WIDTH, D_MODEL), MIX_WIDTH ** -0.5),
        "norm_mix_post": gain(ks[8], D_MODEL),
        "norm_ffn_pre": gain(ks[9], D_MODEL),
        "ffn_w_up": nrm(ks[10], (DEPTH, D_MODEL, 2 * D_FF), D_MODEL ** -0.5),
        "ffn_conv_w": nrm(ks[11], (DEPTH, CONV_K, 2 * D_FF), CONV_K ** -0.5),
        "ffn_conv_b": nrm(ks[12], (DEPTH, 2 * D_FF), 0.02),
        "ffn_w_down": nrm(ks[13], (DEPTH, D_FF, D_MODEL), D_FF ** -0.5),
        "norm_ffn_post": gain(ks[14], D_MODEL),
    }

def reference(x, norm_mix_pre, w_in, pool_w, pool_scale, conv_w, attn_sinks, w_o,
              norm_mix_post, norm_ffn_pre, ffn_w_up, ffn_conv_w, ffn_conv_b, ffn_w_down,
              norm_ffn_post):
    offsets = []
    acc = 0
    for sz in IN_SIZES[:-1]:
        acc += sz
        offsets.append(acc)
    for l in range(DEPTH):
        h = rms_norm(x, norm_mix_pre[l])
        proj = jnp.einsum('bsd,de->bse', h, w_in[l])
        u_pool, g_b, g_c, u_conv, q, k, v = jnp.split(proj, offsets, axis=-1)
        y_pool = pool_mixer(u_pool, pool_w[l], pool_scale[l])
        y_conv = g_b * causal_dwconv(g_c * u_conv, conv_w[l])
        y_attn = swa_sink_attention(q, k, v, attn_sinks[l])
        mix = jnp.einsum('bse,ed->bsd', jnp.concatenate([y_pool, y_conv, y_attn], axis=-1), w_o[l])
        x = x + rms_norm(mix, norm_mix_post[l])
        h = rms_norm(x, norm_ffn_pre[l])
        up = causal_dwconv(jnp.einsum('bsd,df->bsf', h, ffn_w_up[l]), ffn_conv_w[l]) + ffn_conv_b[l]
        gate, val = jnp.split(up, 2, axis=-1)
        ff = jnp.einsum('bsf,fd->bsd', jax.nn.silu(gate) * val, ffn_w_down[l])
        x = x + rms_norm(ff, norm_ffn_post[l])
    return x


_drawn_inputs = setup_inputs


def setup_inputs(seed=0):
    import zlib

    import numpy as np

    out = dict(_drawn_inputs(seed))
    spreads = {}
    factors = {'attn_sinks': 8.0, 'ffn_conv_b': 3.532}
    for name, (base, spread) in spreads.items():
        noise = np.random.default_rng([zlib.crc32(name.encode()), seed]).standard_normal(out[name].shape)
        drawn = base * np.exp(spread * noise) if base else spread * noise
        out[name] = __import__('jax').numpy.asarray(drawn.astype(out[name].dtype))
    for name, factor in factors.items():
        out[name] = (out[name] * factor).astype(out[name].dtype)
    return out
```

```python
from contextlib import ExitStack

import concourse.bass as bass
import numpy as np
from concourse import mybir

F32 = mybir.dt.float32
F32R = mybir.dt.float32r
U32 = mybir.dt.uint32
ALU = mybir.AluOpType
ACT = mybir.ActivationFunctionType
AX = mybir.AxisListType

P = 128
SEQ = 1024
DM = 1024
KD = DM // P
NT = SEQ // P
HALF = 512
IN_W = 1792
NIN = IN_W // P
DFF = 2816
NF = DFF // P
HD = 64
NH = 8
EPS = 1e-6
QK_SCALE = HD ** -0.5
NEG = -1e30
PAD = 16
POOL_WINDOWS = (2, 4, 8, 16)

RAW = 4
SPLIT = 2
W_O0 = NIN
UP0 = W_O0 + KD
DOWN0 = UP0 + 2 * NF
IN_ORDER = (12, 13, 8, 9, 10, 11, 0, 1, 4, 6, 2, 5, 7, 3)
UNIT = [(b, kv) for kv in range(2) for b in range(3)]
UNIT += [(b, kv) for b in range(3, NT) for kv in range(2)]
UNITS = len(UNIT)
SLOT0 = 5
SLOTS = 2 * (NIN - SLOT0)
POOL_SLOT = (8, 10)
TAIL = 4


def build(nc, consts, x, norm_mix_pre, w_in, pool_w, pool_scale, conv_w, attn_sinks, w_o,
          norm_mix_post, norm_ffn_pre, ffn_w_up, ffn_conv_w, ffn_conv_b, ffn_w_down,
          norm_ffn_post, out):
    x2_dram = nc.dram_tensor("x2_dram", (SEQ, DM), F32, kind="Internal").ap()
    x_d, out_d = x[0], out[0]
    w_in_v = w_in[0].rearrange("(k p) c -> p k c", p=P)
    w_up_v = ffn_w_up[0].rearrange("(k p) c -> p k c", p=P)
    NC = consts.shape[1]

    ctx = ExitStack()
    with ctx:
        def alloc(stack, name, shape, dt=F32):
            return stack.enter_context(nc.sbuf_tensor(name, shape, dt))

        def sem(name):
            return ctx.enter_context(nc.semaphore(name))

        wraw = alloc(ctx, "wraw", [P, RAW, DM])
        whi = alloc(ctx, "whi", [P, SPLIT, DM], F32R)
        wlo = alloc(ctx, "wlo", [P, SPLIT, DM], F32R)
        cst = alloc(ctx, "cst", [P, NC])
        par_a = alloc(ctx, "par_a", [P, 4 * NF + 8])
        par_b = alloc(ctx, "par_b", [P, 4 * NF])
        sinks = alloc(ctx, "sinks", [P, NH])
        neg_sinks = alloc(ctx, "neg_sinks", [P, NH])
        sumsq = alloc(ctx, "sumsq", [P, 32])
        meansq = alloc(ctx, "meansq", [P, 32])
        rstd = alloc(ctx, "rstd", [P, 32])
        half_sums = alloc(ctx, "half_sums", [P, 8])
        power = alloc(ctx, "power", [P, 1])
        small = alloc(ctx, "small", [P, 2, 6, 4])
        gain_a = alloc(ctx, "gain_a", [P, DM])

        h1 = ExitStack()
        k_hi = alloc(h1, "k_hi", [P, 2, SEQ], F32R)
        k_lo = alloc(h1, "k_lo", [P, 2, SEQ], F32R)
        mix_pc = alloc(h1, "mix_pc", [P, NT, 4, P])
        q_parts = alloc(h1, "q_parts", [P, NT, NH, P], F32R)
        h1.close()
        h1b = ExitStack()
        alloc(h1b, "under_mix_att", [P, NT * KD * P])
        mix_att = alloc(h1b, "mix_att", [P, NT, 2, 4, P])
        h1b.close()
        h2 = ExitStack()
        h2hi = alloc(h2, "h2hi", [P, NT, KD, P], F32R)
        h2lo = alloc(h2, "h2lo", [P, NT, KD, P], F32R)
        h2.close()
        h3 = ExitStack()
        ff = alloc(h3, "ff", [P, 4, DM])
        w_tail_hi = alloc(h3, "w_tail_hi", [P, TAIL, DM], F32R)
        w_tail_lo = alloc(h3, "w_tail_lo", [P, TAIL, DM], F32R)
        ob = alloc(h3, "ob", [P, 2, DM])
        x2f = alloc(h3, "x2f", [P, 2, DM])
        h3.close()
        h3b = ExitStack()
        a_tail_hi = alloc(h3b, "a_tail_hi", [P, TAIL, HALF], F32R)
        a_tail_lo = alloc(h3b, "a_tail_lo", [P, TAIL, HALF], F32R)
        h3b.close()
        alloc(ctx, "region_h", [P, 2 * NT * KD * P])

        x1 = ExitStack()
        hhi = alloc(x1, "hhi", [P, NT, KD, P], F32R)
        hlo = alloc(x1, "hlo", [P, NT, KD, P], F32R)
        wo_hi = hhi[:].rearrange("p t k c -> p t (k c)")
        wo_lo = hlo[:].rearrange("p t k c -> p t (k c)")
        xa = ExitStack()
        xin = alloc(xa, "xin", [P, 3, DM])
        hrow_a = alloc(xa, "hrow_a", [P, 2, DM])
        xa.close()
        xb_ = ExitStack()
        s_sb = alloc(xb_, "s_sb", [P, 2, 4, P])
        prob = alloc(xb_, "prob", [P, 2, 4, P])
        pt_cur = alloc(xb_, "pt_cur", [P, 4, P])
        pt_prev = alloc(xb_, "pt_prev", [P, 4, P])
        pool_u = alloc(xb_, "pool_u", [P, PAD + SEQ])
        sum_a = alloc(xb_, "sum_a", [P, PAD + SEQ])
        sum_b = alloc(xb_, "sum_b", [P, PAD + SEQ])
        pool_d = alloc(xb_, "pool_d", [P, 2, SEQ])
        v_tok = alloc(xb_, "v_tok", [P, NT, P])
        pool_mat = alloc(xb_, "pool_mat", [P, 2, P])
        neg_big = alloc(xb_, "neg_big", [P, P])
        par_rows = alloc(xb_, "par_rows", [P, 2, P])
        xb_.close()
        xb2 = ExitStack()
        alloc(xb2, "under_conv", [P, 8 * HALF])
        gate_y = alloc(xb2, "gate_y", [P, SEQ])
        conv_in = alloc(xb2, "conv_in", [P, SEQ])
        xb2.close()
        xc = ExitStack()
        gain_b = alloc(xc, "gain_b", [P, DM])
        mhi = alloc(xc, "mhi", [P, 2, KD, P], F32R)
        mlo = alloc(xc, "mlo", [P, 2, KD, P], F32R)
        xres = alloc(xc, "xres", [P, DM])
        x2b = alloc(xc, "x2b", [P, 2, DM])
        hrow_c = alloc(xc, "hrow_c", [P, DM])
        xc.close()
        x1.close()
        x2_ = ExitStack()
        act_raw = alloc(x2_, "act_raw", [P, NF, SEQ])
        yg = alloc(x2_, "yg", [P, 2, SEQ])
        ahi = alloc(x2_, "ahi", [P, 2, HALF], F32R)
        alo = alloc(x2_, "alo", [P, 2, HALF], F32R)
        x2_.close()
        v_chan = pool_d[:, 1, :]

        ps = ctx.enter_context(nc.psum_tensor("ps", [P, 8, HALF], F32))

        def banks(b, n=2):
            return ps[:, b:b + n, :].rearrange("p b c -> p (b c)")

        ident = cst[:, 0:P]
        free_gt = cst[:, P:2 * P]
        cur_ok = cst[:, 2 * P:3 * P]
        prev_ok = cst[:, 3 * P:4 * P]
        inv_cnt = cst[:, 4 * P:4 * P + 2 * PAD].rearrange("p (i c) -> p i c", i=2)
        inv_w = cst[:, 4 * P + 2 * PAD:4 * P + 2 * PAD + 2]
        def pool_sc(i):
            return par_a[:, 4 * NF + i:4 * NF + i + 1]

        def conv_tap(j, c):
            at = 4 * NF + 2 + 2 * j + c
            return par_a[:, at:at + 1]

        def ffn_tap(j, f):
            return par_b[:, bass.ds(f, 1)] if j == 2 else par_a[:, bass.ds(2 * NF * j + f, 1)]

        def ffn_bias(f):
            return par_b[:, bass.ds(2 * NF + f, 1)]

        consts_in = sem("consts_in")
        params_in = sem("params_in")
        pool_w_in = sem("pool_w_in")
        gain_in = sem("gain_pre_in")
        gains_mix_in = sem("gains_mix_in")
        gain_out_in = sem("gain_out_in")
        xin_in = [sem(f"xin_in{i}") for i in range(3)]
        xres_in = sem("xres_in")
        landed = [sem(f"w_landed{i}") for i in range(RAW)]
        x2_saved = [sem("x2_saved0"), sem("x2_saved1")]
        x2_in = [sem("x2_in0"), sem("x2_in1")]
        out_saved = [sem("out_saved0"), sem("out_saved1")]
        w_rounded = sem("w_rounded")
        w_split = sem("w_split")
        set_ = sem("small_consts_set")
        par_turned = sem("params_transposed")
        par_ok = sem("params_ready")
        squared = sem("squares_summed")
        halves_added = sem("half_sums_added")
        ms_ready = sem("meansq_ready")
        rstd_ready = sem("rstd_ready")
        hrow_ready = sem("hrow_ready")
        turned = sem("hrow_transposed")
        ht_rounded = sem("ht_rounded")
        ht_split = sem("ht_split")
        proj_done = sem("proj_done")
        k_rounded = sem("k_rounded")
        q_rounded = sem("q_rounded")
        k_ready = sem("k_ready")
        q_ready = sem("q_ready")
        v_ready = sem("v_chan_ready")
        vt_ready = sem("v_tok_ready")
        scored = sem("scores_done")
        s_copied = sem("scores_copied")
        s_masked = sem("scores_masked")
        negmax = sem("negmax_ready")
        expd = sem("exp_done")
        p_norm = sem("probs_normed")
        p_turned = sem("probs_transposed")
        p_masked = sem("probs_masked")
        pv_done = sem("pv_done")
        pv_out = sem("pv_copied")
        pads = sem("pads_zeroed")
        pool_in = sem("pool_u_ready")
        pool_ready = sem("pool_d_ready")
        pool_mixed = sem("pool_product_done")
        pool_out = sem("pool_out_ready")
        gate_in = sem("g_c_ready")
        conv_v = sem("conv_in_ready")
        conv_y = sem("conv_y_started")
        mix_conv = sem("mix_conv_ready")
        mix_rounded = sem("mix_rounded")
        mix_split = sem("mix_split")
        wo_done = sem("wo_done")
        wo_norm = sem("wo_normed")
        x2_ready = sem("x2_ready")
        up_done = sem("up_done")
        yg_started = sem("gate_started")
        yv_started = sem("value_started")
        silu_done = sem("silu_done")
        up_freed = sem("up_convolved")
        act_ready = sem("act_ready")
        a_rounded = sem("act_rounded")
        a_split = sem("act_split")
        down_tok = sem("down_token_tiles")
        tail_done = sem("down_tail_done")
        ff_act = sem("ff_copied_by_scalar")
        ff_dve = sem("ff_copied_by_vector")
        final = sem("out_tile_ready")
        dve_step = sem("dve_step")

        block = ctx.enter_context(nc.Block())

        use_of = [n + (n > 2) for n in range(NIN)]
        taken = [(ht_split, NT), (v_ready, 1), (k_ready, 2), (vt_ready, 1), (q_ready, 2),
                 (q_ready, 3), (q_ready, 4), (pool_in, 1), (pool_in, 2), (gate_in, 1), (conv_v, 1),
                 (mix_conv, 1), (gate_in, 2), (conv_v, 2)]
        def use_banks(m):
            return 4 if m == 2 else 2 * (m % 2)

        ALL_PROJECTED = NIN + 2

        def turn_banks(i):
            return (4 + 2 * (i % 2) if i < NT else 2 + 4 * (i % 2)), 2

        def wo_bank(t):
            return 4 * (t % 2)

        score_view = banks(4).rearrange("p (i w j) -> p i w j", w=2, j=P)

        NQ = 6

        @block.sync
        def _(sp):
            def buffer_free(n):
                if not isinstance(n, int) or n >= RAW:
                    sp.wait_ge(w_split, n - RAW + 1)

            def load_in(n):
                c = IN_ORDER[n]
                buffer_free(n)
                sp.dma_start(wraw[:, n % RAW, :].rearrange("p (k c) -> p k c", k=KD),
                             w_in_v[:, :, c * P:(c + 1) * P]).then_inc(landed[n % RAW], 16)

            def load_wo(k):
                n = W_O0 + k
                buffer_free(n)
                sp.dma_start(wraw[:, n % RAW, :], w_o[0, k * P:(k + 1) * P, :])\
                  .then_inc(landed[n % RAW], 16)

            def load_up(n, slot, pair, val):
                buffer_free(n)
                sp.dma_start(wraw[:, slot, :].rearrange("p (k c) -> p k c", k=KD),
                             w_up_v[:, :, bass.ds(pair * P + val * DFF, P)])\
                  .then_inc(landed[slot], 16)

            def load_down(n, slot, k):
                buffer_free(n)
                sp.dma_start(wraw[:, slot, :], ffn_w_down[0, bass.ds(k * P, P), :])\
                  .then_inc(landed[slot], 16)

            def load_x(t):
                if t >= 3:
                    sp.wait_ge(hrow_ready, t - 2)
                sp.dma_start(xin[:, t % 3, :], x_d[t * P:(t + 1) * P, :])\
                  .then_inc(xin_in[t % 3], 16)

            load_x(0)
            load_x(1)
            sp.dma_start(gain_a[:, :], norm_mix_pre.broadcast_to([P, DM])).then_inc(gain_in, 16)
            sp.dma_start(cst[:, :], consts).then_inc(consts_in, 16)
            load_in(0)
            load_in(1)
            load_x(2)
            for t in range(3, NT):
                load_x(t)
            for n in range(2, RAW):
                load_in(n)
            taps = ffn_conv_w[0].rearrange("j (f p) -> (j f) p", p=P)
            sp.dma_start(par_rows[0:4 * NF, 0, :], taps[0:4 * NF, :]).then_inc(params_in, 16)
            sp.dma_start(par_rows[4 * NF:4 * NF + 2, 0, :],
                         pool_scale[0].rearrange("(i p) -> i p", p=P)).then_inc(params_in, 16)
            sp.dma_start(par_rows[4 * NF + 2:4 * NF + 8, 0, :],
                         conv_w[0].rearrange("j (i p) -> (j i) p", p=P)).then_inc(params_in, 16)
            sp.dma_start(par_rows[0:2 * NF, 1, :], taps[4 * NF:6 * NF, :])\
              .then_inc(params_in, 16)
            sp.dma_start(par_rows[2 * NF:4 * NF, 1, :],
                         ffn_conv_b[0].rearrange("(f p) -> f p", p=P)).then_inc(params_in, 16)
            sp.dma_start(sinks[:, :], attn_sinks.broadcast_to([P, NH])).then_inc(params_in, 16)
            for n in range(RAW, 6):
                load_in(n)
            sp.wait_ge(hrow_ready, NT)
            sp.dma_start(gain_a[:, :], norm_mix_post.broadcast_to([P, DM]))\
              .then_inc(gains_mix_in, 16)
            for n in range(6, NIN):
                load_in(n)
            for k in range(KD):
                load_wo(k)
            sp.wait_ge(pv_done, UNITS)
            sp.wait_ge(mix_conv, 3)
            sp.wait_ge(pool_out, 2)
            sp.dma_start(gain_b[:, :], norm_ffn_pre.broadcast_to([P, DM]))\
              .then_inc(gains_mix_in, 16)
            sp.dma_start(xres[:, :], x_d[0:P, :]).then_inc(xres_in, 16)
            for n in range(UP0, UP0 + RAW):
                load_up(n, n % RAW, (n - UP0) // 2, (n - UP0) % 2)
            for t in range(NT):
                sp.wait_ge(x2_ready, t + 1)
                sp.dma_start(x2_dram[t * P:(t + 1) * P, :], x2b[:, t % 2, :])\
                  .then_inc(x2_saved[t % 2], 16)
                if t < NT - 1:
                    sp.dma_start(xres[:, :], x_d[(t + 1) * P:(t + 2) * P, :])\
                      .then_inc(xres_in, 16)
            with sp.Fori(0, NF // 2 - 1) as it:
                for j in range(4):
                    load_up(UP0 + RAW + 4 * it + j, (UP0 + j) % RAW, 2 + 2 * it + j // 2, j % 2)
            sp.wait_ge(hrow_ready, 2 * NT)
            sp.dma_start(gain_a[:, :], norm_ffn_post.broadcast_to([P, DM]))\
              .then_inc(gain_out_in, 16)
            for k in range(2):
                load_down(DOWN0 + k, (DOWN0 + k) % RAW, k)
            with sp.Fori(0, (NF - 2) // 4) as it:
                for j in range(4):
                    load_down(DOWN0 + 2 + 4 * it + j, (DOWN0 + 2 + j) % RAW, 2 + 4 * it + j)
            d1 = DOWN0 + NF
            for k in range(NQ):
                load_down(d1 + k, (d1 + k) % RAW, k)
            for q in x2_saved:
                sp.wait_ge(q, 16 * NT // 2)
            sp.wait_ge(ff_act, 1)
            sp.dma_start(x2f[:, 0, :], x2_dram[0:P, :]).then_inc(x2_in[0], 16)
            with sp.Fori(0, 4) as it:
                load_down(d1 + NQ + 4 * it, (d1 + NQ) % RAW, NQ + 4 * it)
                sp.wait_ge(final, it + 1)
                sp.dma_start(out_d[bass.ds(it * P, P), :], ob[:, 0, :]).then_inc(out_saved[0], 16)
                sp.dma_start(x2f[:, 0, :], x2_dram[bass.ds(it * P + P, P), :])\
                  .then_inc(x2_in[0], 16)
                for j in range(1, 4):
                    load_down(d1 + NQ + 4 * it + j, (d1 + NQ + j) % RAW, NQ + 4 * it + j)
            for t in range(4, NT):
                if t < NT - 1:
                    if t >= 5:
                        sp.wait_ge(final, 4 + 2 * (t - 4))
                    sp.dma_start(x2f[:, (t + 1) % 2, :], x2_dram[(t + 1) * P:(t + 2) * P, :])\
                      .then_inc(x2_in[(t + 1) % 2], 16)
                for c in range(2):
                    cols = slice(c * HALF, (c + 1) * HALF)
                    sp.wait_ge(final, 4 + 2 * (t - 4) + c + 1)
                    sp.dma_start(out_d[t * P:(t + 1) * P, cols], ob[:, t % 2, cols])\
                      .then_inc(out_saved[t % 2], 16)
            sp.wait_ge(out_saved[0], 16 * (4 + 2 * 2))
            sp.wait_ge(out_saved[1], 16 * 2 * 2)

        @block.gpsimd
        def _(pool):
            pool.memset(power[:, :], -0.5).then_inc(set_, 1)
            pool.memset(neg_big[:, :], NEG).then_inc(set_, 1)
            pool.memset(pool_mat[:, :, :], 0.0).then_inc(set_, 1)
            def root(i, seen):
                pool.wait_ge(squared, seen)
                pool.tensor_scalar(meansq[:, i:i + 1], sumsq[:, i:i + 1], 1.0 / DM, EPS,
                                   ALU.mult, ALU.add).then_inc(ms_ready, 1)
                pool.wait_ge(ms_ready, seen)
                pool.tensor_tensor(rstd[:, i:i + 1], meansq[:, i:i + 1], power[:, :], ALU.pow)\
                    .then_inc(rstd_ready, 1)

            for i in range(NT):
                root(i, i + 1)
            pool.wait_ge(set_, 3)
            for g in range(4):
                h = HD * (g % 2)
                pool.dma_start(pool_mat[h:h + HD, g // 2, h:h + HD], pool_w[0, g])\
                    .then_inc(pool_w_in, 16)
            pool.wait_ge(ht_split, NT)
            for buf in (pool_u, sum_a, sum_b):
                pool.memset(buf[:, 0:PAD], 0.0).then_inc(pads, 1)
            for i in range(NT, 3 * NT):
                root(i, i + 1)
            for t in range(4):
                root(3 * NT, 3 * NT + 1 + t)
            for t in range(4):
                i = 3 * NT + 4 + t
                pool.wait_ge(squared, 3 * NT + 4 + 2 * t + 2)
                pool.tensor_tensor(sumsq[:, i:i + 1], half_sums[:, 2 * t:2 * t + 1],
                                   half_sums[:, 2 * t + 1:2 * t + 2], ALU.add)\
                    .then_inc(halves_added, 1)
                pool.wait_ge(halves_added, t + 1)
                pool.tensor_scalar(meansq[:, i:i + 1], sumsq[:, i:i + 1], 1.0 / DM, EPS,
                                   ALU.mult, ALU.add).then_inc(ms_ready, 1)
                pool.wait_ge(ms_ready, i + 1)
                pool.tensor_tensor(rstd[:, i:i + 1], meansq[:, i:i + 1], power[:, :], ALU.pow)\
                    .then_inc(rstd_ready, 1)

        @block.scalar
        def _(act):
            def round_weight(base, q, hi, slot):
                n = base + RAW * q
                act.wait_ge(landed[base % RAW], 16 * (base // RAW + 1 + q))
                act.activation(hi[:, slot, :], wraw[:, base % RAW, :], ACT.Copy)\
                   .then_inc(w_rounded, 1)

            def round_ring(n):
                r = n if n < W_O0 else n - KD
                if r >= SPLIT:
                    act.wait_ge(proj_done, use_of[r - SPLIT] + 1 + (r - SPLIT == NIN - 1))
                round_weight(n, 0, whi, r % SPLIT)

            def square_x(t):
                act.wait_ge(xin_in[t % 3], 16 * (t // 3 + 1))
                if t >= 2:
                    act.wait_ge(turned, t - 1)
                act.activation(hrow_a[:, t % 2, :], xin[:, t % 3, :], ACT.Square,
                               accum_out=sumsq[:, t:t + 1]).then_inc(squared, 1)

            def round_h(i, hi):
                act.wait_ge(turned, i + 1)
                act.activation(hi[:, i % NT, :, :].rearrange("p k c -> p (k c)"),
                               banks(*turn_banks(i)), ACT.Copy).then_inc(ht_rounded, 1)

            square_x(0)
            square_x(1)
            round_ring(0)
            round_h(0, hhi)
            round_h(1, hhi)
            square_x(2)
            round_ring(1)
            square_x(3)
            for t in range(2, NT, 2):
                round_h(t, hhi)
                round_h(t + 1, hhi)
                if t + 2 < NT:
                    square_x(t + 2)
                    square_x(t + 3)

            def take(m):
                act.wait_ge(proj_done, m + 1)
                return banks(use_banks(m))

            round_ring(2)
            src = take(0)
            for kv in range(2):
                for e in range(2):
                    last = act.activation(k_hi[e * HD:(e + 1) * HD, kv, :],
                                          src[kv * HD:(kv + 1) * HD, :], ACT.Copy)
                last.then_inc(k_rounded, 1)
            act.activation(v_chan, take(1), ACT.Copy).then_inc(v_ready, 1)
            round_ring(3)

            def round_q(j):
                src = take(use_of[2 + j])
                for e in range(2):
                    act.activation(q_parts[0:HD, :, 2 * j + e, :],
                                   src[e * HD:(e + 1) * HD, :]
                                   .rearrange("p (b c) -> p b c", b=NT), ACT.Copy)\
                       .then_inc(q_rounded, 1)

            round_q(0)
            round_ring(4)
            round_q(1)
            round_ring(5)

            def copy_scores(u):
                act.wait_ge(scored, u + 1)
                act.activation(s_sb[:, u % 2, :, :], score_view[:, :, 1, :], ACT.Copy)\
                   .then_inc(s_copied, 1)

            def exps(u):
                act.wait_ge(negmax, u + 1)
                if u >= 2:
                    act.wait_ge(p_turned, u - 1)
                for i in range(4):
                    act.activation(prob[:, u % 2, i, :], s_sb[:, u % 2, i, :], ACT.Exp,
                                   bias=small[:, u % 2, 1, i:i + 1], scale=QK_SCALE,
                                   accum_out=small[:, u % 2, 3, i:i + 1])
                act.activation(small[:, u % 2, 4, :], small[:, u % 2, 2, :], ACT.Exp)\
                   .then_inc(expd, 1)

            def copy_attended(u):
                act.wait_ge(pv_done, u + 1)
                b, kv = UNIT[u]
                act.activation(mix_att[:, b, kv, 0:2, :].rearrange("p k c -> p (k c)"),
                               ps[:, 7, 0:2 * P], ACT.Copy).then_inc(pv_out, 1)

            def copy_pooled(i):
                act.wait_ge(pool_mixed, i + 1)
                act.activation(mix_pc[:, :, i, :], banks(4).rearrange("p (t c) -> p t c", t=NT),
                               ACT.Copy, scale=pool_sc(i)).then_inc(pool_out, 1)

            def evacuate(s):
                if s < 0:
                    round_q(3)
                elif s < 2:
                    if s == 0:
                        act.wait_ge(pads, 3)
                    else:
                        act.wait_ge(pool_ready, 1)
                    act.activation(pool_u[:, PAD:], take(7 + s), ACT.Copy).then_inc(pool_in, 1)
                elif s % 3 == 2:
                    if s == 2:
                        act.wait_ge(pool_ready, 2)
                    if s == 5:
                        act.wait_ge(mix_conv, 1)
                    act.activation(gate_y[:, :], take(7 + s), ACT.Copy).then_inc(gate_in, 1)

            def start_conv(c):
                act.wait_ge(conv_v, c + 1)
                act.activation(gate_y[:, :], conv_in[:, :], ACT.Copy,
                               scale=conv_tap(2, c)).then_inc(conv_y, 1)

            act.wait_ge(par_ok, 3)

            for u in range(UNITS):
                if u >= 2:
                    copy_attended(u - 2)
                copy_scores(u)
                if u == 0:
                    round_q(2)
                if u % 2 == 0:
                    if u >= 2 and u != 8:
                        evacuate(u // 2 - 2)
                    round_ring(SLOT0 + u // 2 + 1)
                if u == 11:
                    start_conv(0)
                exps(u)
                if u in POOL_SLOT:
                    copy_pooled(POOL_SLOT.index(u))
                if u == 8:
                    evacuate(2)

            def round_wo(k):
                round_weight(W_O0 + k, 0, wo_hi, k)

            def round_mix(t):
                if t >= 2:
                    act.wait_ge(wo_done, t - 1)
                act.activation(mhi[:, t % 2, 0:4, :], mix_pc[:, t, :, :], ACT.Copy)
                act.activation(mhi[:, t % 2, 4:8, :].rearrange("p (v k) c -> p v (k c)", v=2),
                               mix_att[:, t, :, 0:2, :].rearrange("p v k c -> p v (k c)"),
                               ACT.Copy).then_inc(mix_rounded, 1)

            copy_attended(UNITS - 2)
            start_conv(1)
            act.wait_ge(mix_conv, 2)
            act.wait_ge(pool_out, 2)
            act.wait_ge(pv_out, 4)
            act.wait_ge(p_turned, UNITS)
            round_mix(0)
            act.wait_ge(proj_done, ALL_PROJECTED - 1)
            round_wo(0)
            round_wo(1)
            copy_attended(UNITS - 1)
            for k in range(2, KD):
                if k == KD // 2:
                    act.wait_ge(proj_done, ALL_PROJECTED)
                round_wo(k)
            act.wait_ge(mix_conv, 3)
            act.wait_ge(pv_out, UNITS)
            round_mix(1)
            for t in range(NT):
                src = wo_bank(t)
                act.wait_ge(wo_done, t + 1)
                if t >= 2:
                    act.wait_ge(x2_saved[t % 2], 16 * (t // 2))
                act.activation(x2b[:, t % 2, :], banks(src), ACT.Square,
                               accum_out=sumsq[:, NT + 2 * t:NT + 2 * t + 1]).then_inc(squared, 1)
                if t + 2 < NT:
                    round_mix(t + 2)
                if t >= 1:
                    round_h(NT + t - 1, h2hi)
                act.wait_ge(x2_ready, t + 1)
                act.activation(hrow_c[:, :], x2b[:, t % 2, :], ACT.Square,
                               accum_out=sumsq[:, NT + 2 * t + 1:NT + 2 * t + 2])\
                   .then_inc(squared, 1)
                if t in (4, 5):
                    round_ring(UP0 + t - 4)
            round_h(2 * NT - 1, h2hi)

            def up_step(q, j, first=False):
                pair = 2 * q + j
                base = UP0 + 2 + 2 * j
                act.wait_ge(up_done, 2 * pair + 1)
                round_weight(base, q, whi, 0)
                if not first:
                    act.wait_ge(act_ready, pair - 1)
                act.activation(yg[:, j, :], banks(4 * j), ACT.Identity, bias=ffn_bias(pair),
                               scale=ffn_tap(2, pair)).then_inc(yg_started, 1)
                act.wait_ge(up_done, 2 * pair + 2)
                round_weight(base + 1, q, whi, 1)
                act.activation(act_raw[:, bass.ds(pair, 1), :].rearrange("p o c -> p (o c)"),
                               banks(4 * j + 2), ACT.Identity, bias=ffn_bias(pair + NF),
                               scale=ffn_tap(2, pair + NF)).then_inc(yv_started, 1)
                act.wait_ge(up_freed, 2 * pair + 1)
                act.activation(yg[:, j, :], yg[:, j, :], ACT.Silu).then_inc(silu_done, 1)

            def act_part(k, half):
                return act_raw[:, bass.ds(k, 1), half * HALF:(half + 1) * HALF]\
                    .rearrange("p o c -> p (o c)")

            def round_act(k, half, hi, slot):
                if half == 0:
                    act.wait_ge(act_ready, k + 1)
                act.activation(hi[:, slot, :], act_part(k, half), ACT.Copy).then_inc(a_rounded, 1)

            for q in x2_saved:
                act.wait_ge(q, 16 * NT // 2)
            up_step(0, 0, True)
            up_step(0, 1, True)
            with act.Fori(0, NF // 2 - 2) as it:
                for j in range(2):
                    up_step(it + 1, j)
            up_step(NF // 2 - 1, 0)
            for k in range(2):
                round_act(k, 0, ahi, k)
            up_step(NF // 2 - 1, 1)

            def down_step(base, q, k, half):
                act.wait_ge(down_tok, 4 * (base - DOWN0 + RAW * q - 1))
                round_weight(base, q, whi, base % 2)
                round_act(k, half, ahi, base % 2)

            with act.Fori(0, (NF - 2) // 4) as it:
                for j in range(4):
                    down_step(DOWN0 + 2 + j, it, 2 + 4 * it + j, 0)
            d1 = DOWN0 + NF
            down_step(d1, 0, 0, 1)
            for t in (0, 2):
                act.wait_ge(down_tok, 4 * (NF - 1) + t + 1)
                act.activation(ff[:, t, :], banks(2 * t), ACT.Copy).then_inc(ff_act, 1)
            down_step(d1 + 1, 0, 1, 1)
            act.wait_ge(ff_dve, 2)
            act.wait_ge(ff_act, 2)
            with act.Fori(0, 4) as it:
                for j in range(4):
                    down_step(d1 + 2 + j, it, 2 + 4 * it + j, 1)
                    if j == 0:
                        act.activation(ob[:, 0, :], ff[:, bass.ds(it, 1), :]
                                       .rearrange("p o c -> p (o c)"), ACT.Square,
                                       accum_out=sumsq[:, 3 * NT:3 * NT + 1]).then_inc(squared, 1)
                act.wait_ge(out_saved[0], 16 * it + 16)
            for j in range(TAIL):
                round_weight(d1 + NF - TAIL + j, 0, w_tail_hi, j)
                round_act(NF - TAIL + j, 1, a_tail_hi, j)
            for t in range(4):
                for c in range(2):
                    act.wait_ge(tail_done, 2 * t + c + 1)
                    if t or c:
                        act.wait_ge(squared, 3 * NT + 4 + 2 * t + c)
                    act.activation(yg[:, 0, 0:HALF], ps[:, 2 * t + c, :], ACT.Square,
                                   accum_out=half_sums[:, 2 * t + c:2 * t + c + 1])\
                       .then_inc(squared, 1)

        @block.vector
        def _(dve):
            steps = [0]

            def finish_step(instruction):
                instruction.then_inc(dve_step, 1)
                steps[0] = steps[0] + 1
                dve.wait_ge(dve_step, steps[0])

            def low_weight(base, q, hi, lo, slot):
                n = base + RAW * q
                dve.wait_ge(w_rounded, n + 1)
                dve.tensor_tensor(lo[:, slot, :], wraw[:, base % RAW, :], hi[:, slot, :],
                                  ALU.subtract).then_inc(w_split, 1)

            def low_ring(n):
                r = n if n < W_O0 else n - KD
                low_weight(n, 0, whi, wlo, r % SPLIT)

            def norm_x(t):
                if t == 0:
                    dve.wait_ge(gain_in, 16)
                dve.wait_ge(rstd_ready, t + 1)
                dve.scalar_tensor_tensor(hrow_a[:, t % 2, :], xin[:, t % 3, :], rstd[:, t:t + 1],
                                         gain_a[:, :], ALU.mult, ALU.mult)\
                   .then_inc(hrow_ready, 1)

            def low_h(i, hi, lo):
                dve.wait_ge(ht_rounded, i + 1)
                flat = "p k c -> p (k c)"
                dve.tensor_tensor(lo[:, i % NT, :, :].rearrange(flat), banks(*turn_banks(i)),
                                  hi[:, i % NT, :, :].rearrange(flat), ALU.subtract)\
                   .then_inc(ht_split, 1)

            norm_x(0)
            norm_x(1)
            low_ring(0)
            low_h(0, hhi, hlo)
            low_h(1, hhi, hlo)
            norm_x(2)
            low_ring(1)
            norm_x(3)
            for t in range(2, NT, 2):
                low_h(t, hhi, hlo)
                low_h(t + 1, hhi, hlo)
                if t + 2 < NT:
                    norm_x(t + 2)
                    norm_x(t + 3)

            def take(m):
                dve.wait_ge(proj_done, m + 1)
                return banks(use_banks(m))

            low_ring(2)
            src = take(0)
            for kv in range(2):
                dve.wait_ge(k_rounded, kv + 1)
                for e in range(2):
                    rows = slice(e * HD, (e + 1) * HD)
                    last = dve.tensor_tensor(k_lo[rows, kv, :], src[kv * HD:(kv + 1) * HD, :],
                                             k_hi[rows, kv, :], ALU.subtract)
                last.then_inc(k_ready, 1)
            dve.wait_ge(params_in, 16 * 6)
            dve.tensor_scalar(neg_sinks[:, :], sinks[:, :], -1.0, None, ALU.mult)\
               .then_inc(par_ok, 1)
            dve.wait_ge(par_turned, 1)
            dve.tensor_copy(par_a[:, :], ps[:, 6, 0:4 * NF + 8]).then_inc(par_ok, 1)
            dve.tensor_copy(par_b[:, :], ps[:, 7, 0:4 * NF]).then_inc(par_ok, 1)
            dve.wait_ge(par_ok, 3)
            dve.wait_ge(set_, 3)
            low_ring(3)

            def low_q(j):
                src = take(use_of[2 + j])
                for e in range(2):
                    dve.wait_ge(q_rounded, 2 * j + e + 1)
                    last = dve.tensor_tensor(q_parts[HD:P, :, 2 * j + e, :],
                                             src[e * HD:(e + 1) * HD, :]
                                             .rearrange("p (b c) -> p b c", b=NT),
                                             q_parts[0:HD, :, 2 * j + e, :], ALU.subtract)
                last.then_inc(q_ready, 1)

            low_q(0)
            low_ring(4)
            dve.tensor_copy(v_tok[:, :, :].rearrange("p b c -> p (b c)"), take(3))\
               .then_inc(vt_ready, 1)
            low_q(1)
            low_ring(5)

            sink_view = [x[:, :].rearrange("p (v g e) -> p v e g", v=2, g=2)
                         for x in (sinks, neg_sinks)]

            def quad(u, row):
                return small[:, u % 2, row, :].rearrange("p (e g) -> p e g", e=2)

            def over_keys(x):
                return x.rearrange("p (h o) -> p h o", o=1).broadcast_to([P, 4, P])

            def over_heads(x):
                return x.rearrange("p (o j) -> p o j", o=1).broadcast_to([P, 4, P])

            def mask_scores(u):
                b, kv = UNIT[u]
                s = s_sb[:, u % 2, :, :]
                dve.wait_ge(s_copied, u + 1)
                dve.copy_predicated(s, over_heads(free_gt.bitcast(U32)),
                                    score_view[:, :, 0, :] if b else over_heads(neg_big[:, :]))\
                   .then_inc(s_masked, 1)
                dve.wait_ge(s_masked, u + 1)
                finish_step(dve.reduce_max(small[:, u % 2, 0, :], s, AX.X))
                finish_step(dve.scalar_tensor_tensor(quad(u, 1), quad(u, 0), -QK_SCALE,
                                                   sink_view[1][:, kv], ALU.mult, ALU.min))
                dve.tensor_tensor(quad(u, 2), quad(u, 1), sink_view[0][:, kv], ALU.add)\
                   .then_inc(negmax, 1)

            def norm_probs(u):
                dve.wait_ge(expd, u + 1)
                finish_step(dve.tensor_tensor(small[:, u % 2, 5, :], small[:, u % 2, 3, :],
                                            small[:, u % 2, 4, :], ALU.add))
                finish_step(dve.reciprocal(small[:, u % 2, 0, :], small[:, u % 2, 5, :]))
                p = prob[:, u % 2, :, :]
                dve.tensor_tensor(p, p, over_keys(small[:, u % 2, 0, :]), ALU.mult)\
                   .then_inc(p_norm, 1)

            def mask_probs(u):
                dve.wait_ge(p_turned, u + 1)
                if u >= 1:
                    dve.wait_ge(pv_done, u)
                turned_p = ps[:, 6, :].rearrange("p (h q) -> p h q", h=4)
                last = dve.tensor_tensor(pt_cur[:, :, :], turned_p, over_heads(cur_ok), ALU.mult)
                if UNIT[u][0]:
                    last = dve.tensor_tensor(pt_prev[:, :, :], turned_p, over_heads(prev_ok),
                                             ALU.mult)
                last.then_inc(p_masked, 1)

            def trailing_sum(dst, src, by, rows=slice(0, P)):
                finish_step(dve.tensor_tensor(dst[rows, PAD:], src[rows, PAD:],
                                            src[rows, PAD - by:PAD + SEQ - by], ALU.add))

            def pool_sums(i):
                dve.wait_ge(pool_in, i + 1)
                if i == 0:
                    dve.wait_ge(pads, 3)
                    trailing_sum(sum_a, pool_u, 1)
                    trailing_sum(sum_b, sum_a, 2, slice(HD, P))
                else:
                    trailing_sum(sum_a, pool_u, 1)
                    trailing_sum(sum_b, sum_a, 2)

            def longer_sums():
                trailing_sum(sum_a, sum_b, 4)
                trailing_sum(sum_b, sum_a, 8, slice(HD, P))

            def pool_means(i):
                halves = ((sum_a, slice(0, HD)), (sum_b, slice(HD, P)))
                for total, rows in halves:
                    ins = dve.scalar_tensor_tensor(
                        pool_d[rows, i, PAD:], total[rows, 2 * PAD:], inv_w[rows, i:i + 1],
                        pool_u[rows, 2 * PAD:], ALU.mult, ALU.subtract)
                for total, rows in halves:
                    ins = dve.tensor_tensor(pool_d[rows, i, 0:PAD], total[rows, PAD:2 * PAD],
                                            inv_cnt[rows, i, :], ALU.mult)
                finish_step(ins)
                dve.tensor_tensor(pool_d[:, i, 0:PAD], pool_d[:, i, 0:PAD],
                                  pool_u[:, PAD:2 * PAD], ALU.subtract).then_inc(pool_ready, 1)

            def conv_step(s):
                c = (s - 2) // 3
                if s % 3 == 0:
                    dve.wait_ge(gate_in, c + 1)
                    dve.tensor_tensor(conv_in[:, :], take(7 + s), gate_y[:, :], ALU.mult)\
                       .then_inc(conv_v, 1)
                if s == 4:
                    gate_conv(0, take(7 + s), slice(0, NT))

            def gate_conv(c, src, tiles):
                as_tiles = "p (t c) -> p t c"
                dve.tensor_tensor(mix_pc[:, tiles, 2 + c, :],
                                  src.rearrange(as_tiles, t=NT)[:, tiles, :],
                                  gate_y[:, :].rearrange(as_tiles, t=NT)[:, tiles, :], ALU.mult)\
                   .then_inc(mix_conv, 1)

            def conv_taps(c):
                dve.wait_ge(conv_y, c + 1)
                for j, by in ((1, 1), (0, 2)):
                    finish_step(dve.scalar_tensor_tensor(
                        gate_y[:, by:], conv_in[:, :SEQ - by], conv_tap(j, c), gate_y[:, by:],
                        ALU.mult, ALU.add))

            def mixer_work(u):
                s = u // 2 - 2
                if u == 8:
                    pool_means(1)
                if u % 2 == 0:
                    if s in (0, 1):
                        pool_sums(s)
                    elif s >= 2:
                        conv_step(s)
                elif s == 0:
                    pool_means(0)
                elif s == 1:
                    longer_sums()
                elif s % 3 == 0 and s > 0:
                    conv_taps((s - 2) // 3)

            for u in range(UNITS):
                mask_scores(u)
                if u == 0:
                    low_q(2)
                if u >= 1:
                    mask_probs(u - 1)
                if u == 2:
                    low_q(3)
                    norm_probs(u)
                if u % 2 == 0:
                    low_ring(SLOT0 + u // 2 + 1)
                if 4 <= u < 9:
                    norm_probs(u)
                mixer_work(u)
                if u in (0, 1, 3) or u >= 9:
                    norm_probs(u)

            def low_wo(k):
                low_weight(W_O0 + k, 0, wo_hi, wo_lo, k)

            def low_mix(t):
                dve.wait_ge(mix_rounded, t + 1)
                dve.tensor_tensor(mlo[:, t % 2, 0:4, :], mix_pc[:, t, :, :],
                                  mhi[:, t % 2, 0:4, :], ALU.subtract)
                parts = [m[:, t % 2, 4:8, :].rearrange("p (v k) c -> p v (k c)", v=2)
                         for m in (mlo, mhi)]
                dve.tensor_tensor(parts[0], mix_att[:, t, :, 0:2, :]
                                  .rearrange("p v k c -> p v (k c)"), parts[1], ALU.subtract)\
                   .then_inc(mix_split, 1)

            conv_step(6)
            mask_probs(UNITS - 1)
            conv_taps(1)
            for c in range(2):
                dve.wait_ge(proj_done, NIN + 1 + c)
                gate_conv(1, banks(0), slice(4 * c, 4 * c + 4))
                if c == 0:
                    low_mix(0)
                    for k in range(2):
                        low_wo(k)
            for k in range(2, KD):
                low_wo(k)
            low_mix(1)
            dve.wait_ge(gains_mix_in, 32)
            for t in range(NT):
                rows = x2b[:, t % 2, :]
                i = NT + 2 * t
                dve.wait_ge(rstd_ready, i + 1)
                dve.scalar_tensor_tensor(rows, banks(wo_bank(t)), rstd[:, i:i + 1], gain_a[:, :],
                                         ALU.mult, ALU.mult).then_inc(wo_norm, 1)
                dve.wait_ge(wo_norm, t + 1)
                dve.wait_ge(xres_in, 16 * (t + 1))
                dve.tensor_tensor(rows, rows, xres[:, :], ALU.add).then_inc(x2_ready, 1)
                if t + 2 < NT:
                    low_mix(t + 2)
                if t >= 1:
                    low_h(NT + t - 1, h2hi, h2lo)
                dve.wait_ge(rstd_ready, i + 2)
                dve.scalar_tensor_tensor(hrow_c[:, :], rows, rstd[:, i + 1:i + 2], gain_b[:, :],
                                         ALU.mult, ALU.mult).then_inc(hrow_ready, 1)
                if t in (4, 5):
                    low_ring(UP0 + t - 4)
            low_h(2 * NT - 1, h2hi, h2lo)

            def add_taps(y, src, f):
                finish_step(dve.scalar_tensor_tensor(y[:, 1:], src[:, :SEQ - 1], ffn_tap(1, f),
                                                   y[:, 1:], ALU.mult, ALU.add))
                dve.scalar_tensor_tensor(y[:, 2:], src[:, :SEQ - 2], ffn_tap(0, f), y[:, 2:],
                                         ALU.mult, ALU.add).then_inc(up_freed, 1)

            def up_step(q, j):
                pair = 2 * q + j
                base = UP0 + 2 + 2 * j
                low_weight(base, q, whi, wlo, 0)
                dve.wait_ge(yg_started, pair + 1)
                add_taps(yg[:, j, :], banks(4 * j), pair)
                low_weight(base + 1, q, whi, wlo, 1)
                dve.wait_ge(yv_started, pair + 1)
                value = act_raw[:, bass.ds(pair, 1), :].rearrange("p o c -> p (o c)")
                add_taps(value, banks(4 * j + 2), pair + NF)
                dve.wait_ge(up_freed, 2 * pair + 2)
                dve.wait_ge(silu_done, pair + 1)
                dve.tensor_tensor(value, yg[:, j, :], value, ALU.mult).then_inc(act_ready, 1)

            up_step(0, 0)
            up_step(0, 1)
            def low_act(k, kk, half, hi, lo, slot):
                dve.wait_ge(a_rounded, kk + 1)
                dve.tensor_tensor(lo[:, slot, :],
                                  act_raw[:, bass.ds(k, 1), half * HALF:(half + 1) * HALF]
                                  .rearrange("p o c -> p (o c)"), hi[:, slot, :], ALU.subtract)\
                   .then_inc(a_split, 1)

            start = steps[0]
            with dve.Fori(0, NF // 2 - 2) as it:
                steps[0] = start + 4 * it
                for j in range(2):
                    up_step(it + 1, j)
            steps[0] = start + 4 * (NF // 2 - 2)
            up_step(NF // 2 - 1, 0)
            for k in range(2):
                low_act(k, k, 0, ahi, alo, k)
            up_step(NF // 2 - 1, 1)

            def down_step(base, q, k, half):
                low_weight(base, q, whi, wlo, base % 2)
                low_act(k, base - DOWN0 + RAW * q, half, ahi, alo, base % 2)

            with dve.Fori(0, (NF - 2) // 4) as it:
                for j in range(4):
                    down_step(DOWN0 + 2 + j, it, 2 + 4 * it + j, 0)
            d1 = DOWN0 + NF
            down_step(d1, 0, 0, 1)
            for t in (1, 3):
                dve.wait_ge(down_tok, 4 * (NF - 1) + t + 1)
                dve.tensor_copy(ff[:, t, :], banks(2 * t)).then_inc(ff_dve, 1)
            down_step(d1 + 1, 0, 1, 1)

            def finish(src, col, seen, slot, x2_seen):
                dve.wait_ge(rstd_ready, seen)
                finish_step(dve.scalar_tensor_tensor(ob[:, slot, :], src, rstd[:, col:col + 1],
                                                   gain_a[:, :], ALU.mult, ALU.mult))
                dve.wait_ge(x2_in[slot], x2_seen)
                dve.tensor_tensor(ob[:, slot, :], ob[:, slot, :], x2f[:, slot, :], ALU.add)\
                   .then_inc(final, 1)

            dve.wait_ge(gain_out_in, 16)
            dve.wait_ge(ff_act, 2)
            dve.wait_ge(ff_dve, 2)
            start = steps[0]
            with dve.Fori(0, 4) as it:
                steps[0] = start + it
                for j in range(4):
                    down_step(d1 + 2 + j, it, 2 + 4 * it + j, 1)
                    if j == 0:
                        finish(ff[:, bass.ds(it, 1), :].rearrange("p o c -> p (o c)"),
                               3 * NT, 3 * NT + 1 + it, 0, 16 * it + 16)
                dve.wait_ge(out_saved[0], 16 * it + 16)
            steps[0] = start + 4
            for j in range(TAIL):
                low_weight(d1 + NF - TAIL + j, 0, w_tail_hi, w_tail_lo, j)
                low_act(NF - TAIL + j, 2 * NF - TAIL + j, 1, a_tail_hi, a_tail_lo, j)
            for t in range(4):
                i, slot = 3 * NT + 4 + t, t % 2
                for c in range(2):
                    cols = slice(c * HALF, (c + 1) * HALF)
                    dve.wait_ge(squared, 3 * NT + 4 + 2 * t + c + 1)
                    if t == 2 and c == 0:
                        dve.wait_ge(out_saved[0], 16 * 6)
                    if t == 3 and c == 0:
                        dve.wait_ge(out_saved[1], 32)
                    last = dve.tensor_tensor(ob[:, slot, cols], ps[:, 2 * t + c, :],
                                             gain_a[:, cols], ALU.mult)
                finish_step(last)
                dve.wait_ge(rstd_ready, i + 1)
                dve.wait_ge(x2_in[slot], (80, 16, 96, 32)[t])
                for c in range(2):
                    cols = slice(c * HALF, (c + 1) * HALF)
                    dve.scalar_tensor_tensor(ob[:, slot, cols], ob[:, slot, cols],
                                             rstd[:, i:i + 1], x2f[:, slot, cols],
                                             ALU.mult, ALU.add).then_inc(final, 1)

        @block.tensor
        def _(pe):
            def product(acc, w_hi, w_lo, x_hi, x_lo, first, last, looped=False):
                pe.matmul(acc, w_hi, x_hi, start=first, stop=False, skip_group_check=looped)
                pe.matmul(acc, w_hi, x_lo, start=False, stop=False, skip_group_check=looped)
                return pe.matmul(acc, w_lo, x_hi, start=False, stop=last,
                                 skip_group_check=looped)

            def turn(i, rows):
                pe.wait_ge(hrow_ready, i + 1)
                b, _ = turn_banks(i)
                for k in range(KD):
                    last = pe.transpose(ps[:, b + k // 4, (k % 4) * P:(k % 4 + 1) * P],
                                        rows[:, k * P:(k + 1) * P], ident)
                last.then_inc(turned, 1)

            def turn_x(t):
                if t >= 2:
                    pe.wait_ge(ht_split, t - 1)
                turn(t, hrow_a[:, t % 2, :])

            def channels(acc_bank, slot, hi, lo, tiles, ks=range(KD)):
                acc = ps[:, acc_bank, :].rearrange("p (t c) -> p t c", t=4)
                acc = acc[:, tiles.start % 4:(tiles.stop - 1) % 4 + 1, :]
                for k in ks:
                    w = slice(k * P, (k + 1) * P)
                    last = product(acc, whi[:, slot, w], wlo[:, slot, w],
                                   hi[:, tiles, k, :], lo[:, tiles, k, :], k == 0, k == KD - 1)
                return last

            def half_of(c):
                return slice(4 * c, 4 * c + 4)

            def project(m, n, c, ks=range(KD)):
                return channels(use_banks(m) + c, n % SPLIT, hhi, hlo, half_of(c), ks)

            def keep_clock(n):
                for _ in range(n):
                    pe.matmul(ps[:, 0, 0:2 * P], pool_mat[:, 0, :], pool_mat[:, :, :],
                              start=True, stop=True)

            pe.wait_ge(set_, 3)
            keep_clock(11)
            pe.wait_ge(consts_in, 16)
            turn_x(0)
            turn_x(1)
            keep_clock(4)
            for pair in range(NT // 2):
                tiles = slice(2 * pair, 2 * pair + 2)
                pe.wait_ge(ht_split, 2 * pair + 2)
                for n in range(2):
                    if pair == 0:
                        pe.wait_ge(w_split, n + 1)
                    last = channels(2 * n + pair // 2, n, hhi, hlo, tiles)
                    if n == 0 and pair < NT // 2 - 1:
                        turn_x(2 * pair + 2)
                        turn_x(2 * pair + 3)
                    if pair == NT // 2 - 1:
                        last.then_inc(proj_done, 1)
            pe.wait_ge(params_in, 16 * 6)
            pe.transpose(ps[:, 6, 0:4 * NF + 8], par_rows[0:4 * NF + 8, 0, :],
                         ident[0:4 * NF + 8, 0:4 * NF + 8])
            pe.transpose(ps[:, 7, 0:4 * NF], par_rows[0:4 * NF, 1, :],
                         ident[0:4 * NF, 0:4 * NF]).then_inc(par_turned, 1)

            def set_free(m):
                pe.wait_ge(*taken[m - 2])

            def whole_tile(n):
                m = use_of[n]
                set_free(m)
                pe.wait_ge(w_split, n + 1)
                project(m, n, 0)
                project(m, n, 1).then_inc(proj_done, 1)

            whole_tile(2)
            set_free(3)
            for b in range(NT):
                last = pe.transpose(ps[:, 2 + b // 4, (b % 4) * P:(b % 4 + 1) * P],
                                    v_chan[:, b * P:(b + 1) * P], ident)
            last.then_inc(proj_done, 1)
            for n in range(3, SLOT0):
                whole_tile(n)

            def score(u):
                b, kv = UNIT[u]
                if u >= 1:
                    pe.wait_ge(s_masked, u)
                if u - 1 in POOL_SLOT:
                    pe.wait_ge(pool_out, POOL_SLOT.index(u - 1) + 1)
                if u == 0:
                    pe.wait_ge(k_ready, 2)
                    pe.wait_ge(q_ready, 2)
                if u == 3:
                    pe.wait_ge(q_ready, 4)
                first = max(b - 1, 0)
                keys = slice(first * P, (b + 1) * P)
                for e in range(2):
                    for g in range(2):
                        at = g * 2 * P + (first - b + 1) * P
                        acc = ps[:, 4 + e, at:(g + 1) * 2 * P]
                        q = q_parts[:, b, 4 * kv + 2 * g + e, :]
                        pe.matmul(acc, q, k_hi[:, kv, keys], start=True, stop=False)
                        last = pe.matmul(acc, q, k_lo[:, kv, keys], start=False, stop=True)
                last.then_inc(scored, 1)

            def turn_probs(u):
                pe.wait_ge(p_norm, u + 1)
                if u >= 1:
                    pe.wait_ge(p_masked, u)
                for i in range(4):
                    last = pe.transpose(ps[:, 6, i * P:(i + 1) * P], prob[:, u % 2, i, :], ident)
                last.then_inc(p_turned, 1)

            def attend(u):
                b, kv = UNIT[u]
                pe.wait_ge(p_masked, u + 1)
                if u == 0:
                    pe.wait_ge(vt_ready, 1)
                if u >= 1:
                    pe.wait_ge(pv_out, u)
                cols = slice(kv * HD, (kv + 1) * HD)
                for e in range(2):
                    acc = ps[e * HD:(e + 1) * HD, 7, 0:2 * P]
                    heads = slice(2 * e, 2 * e + 2)
                    last = pe.matmul(acc, v_tok[:, b, cols],
                                     pt_cur[:, heads, :].rearrange("p h q -> p (h q)"),
                                     start=True, stop=b == 0)
                    if b:
                        last = pe.matmul(acc, v_tok[:, b - 1, cols],
                                         pt_prev[:, heads, :].rearrange("p h q -> p (h q)"),
                                         start=False, stop=True)
                last.then_inc(pv_done, 1)

            def pool_product(i):
                if i == 0:
                    pe.wait_ge(pool_w_in, 64)
                pe.wait_ge(pool_ready, i + 1)
                pe.wait_ge(s_masked, POOL_SLOT[i] + 1)
                for c in range(2):
                    last = pe.matmul(ps[:, 4 + c, :], pool_mat[:, i, :],
                                     pool_d[:, i, c * HALF:(c + 1) * HALF],
                                     start=True, stop=True)
                last.then_inc(pool_mixed, 1)

            for u in range(SLOTS):
                n, c = SLOT0 + u // 2, u % 2
                if u < UNITS:
                    score(u)
                if 2 <= u <= UNITS:
                    turn_probs(u - 1)
                if c == 0:
                    set_free(use_of[n])
                    pe.wait_ge(w_split, n + 1)
                project(use_of[n], n, c, range(0, 4))
                if u == 1:
                    turn_probs(0)
                if u in POOL_SLOT:
                    pool_product(POOL_SLOT.index(u))
                last = project(use_of[n], n, c, range(4, KD))
                if c == 1 or n == NIN - 1:
                    last.then_inc(proj_done, 1)
                if 1 <= u < UNITS:
                    attend(u - 1)
            attend(UNITS - 1)

            def out_project(t):
                pe.wait_ge(mix_split, t + 1)
                if t == 0:
                    pe.wait_ge(mix_conv, 3)
                if t == 1:
                    pe.wait_ge(s_masked, UNITS)
                if t >= 2:
                    pe.wait_ge(wo_norm, t - 1)
                for k in range(KD):
                    if t == 0:
                        pe.wait_ge(w_split, W_O0 + k + 1)
                    for c in range(2):
                        cols = slice(c * HALF, (c + 1) * HALF)
                        last = product(ps[:, wo_bank(t) + c, :], mhi[:, t % 2, k, :],
                                       mlo[:, t % 2, k, :], wo_hi[:, k, cols], wo_lo[:, k, cols],
                                       k == 0, k == KD - 1)
                last.then_inc(wo_done, 1)

            def turn_x2(t):
                if t == 0:
                    pe.wait_ge(conv_v, 2)
                elif t == 1:
                    pe.wait_ge(pv_out, UNITS)
                else:
                    pe.wait_ge(ht_split, NT + t - 1)
                turn(NT + t, hrow_c[:, :])

            for t in range(NT):
                out_project(t)
                if t >= 1:
                    turn_x2(t - 1)

            def up(i, c, ks=range(KD)):
                return channels(2 * (i % 4) + c, i % 2, h2hi, h2lo, half_of(c), ks)

            pe.wait_ge(wo_norm, NT - 1)
            pe.wait_ge(ht_split, NT + 4)
            pe.wait_ge(w_split, UP0 + 1)
            up(0, 0)
            pe.wait_ge(ht_split, 2 * NT - 1)
            pe.wait_ge(w_split, UP0 + 2)
            up(1, 0, range(0, 2))
            turn_x2(NT - 1)
            up(1, 0, range(2, KD))
            pe.wait_ge(ht_split, 2 * NT)
            up(0, 1).then_inc(up_done, 1)
            up(1, 1).then_inc(up_done, 1)
            for i in range(2, 4):
                pe.wait_ge(w_split, UP0 + i + 1)
                up(i, 0)
                up(i, 1).then_inc(up_done, 1)
            with pe.Fori(0, NF // 2 - 1) as it:
                for j in range(4):
                    pe.wait_ge(w_split, UP0 + 4 * it + 5 + j)
                    pe.wait_ge(up_freed, 4 * it + j + 1)
                    up(j, 0)
                    up(j, 1).then_inc(up_done, 1)

            def down_ring(t, k, first=False, last_k=False):
                tok, slot = slice(t * P, (t + 1) * P), k % 2
                for c in range(2):
                    cols = slice(c * HALF, (c + 1) * HALF)
                    last = product(ps[:, 2 * t + c, :], ahi[:, slot, tok], alo[:, slot, tok],
                                   whi[:, slot, cols], wlo[:, slot, cols], first, last_k, True)
                return last

            def down_start(kk, order, banks_free):
                for k, t in order:
                    pe.wait_ge(w_split, DOWN0 + kk + k + 1)
                    pe.wait_ge(a_split, kk + k + 1)
                    if k == 0:
                        banks_free(t)
                    last = down_ring(t, k, first=k == 0)
                    if t >= 2:
                        last.then_inc(down_tok, 2)

            down_start(0, ((0, 0), (0, 1), (1, 0), (1, 1), (0, 2), (0, 3), (1, 2), (1, 3)),
                       lambda t: pe.wait_ge(up_freed, 2 * NF - 2 + 2 * (t // 2)))
            with pe.Fori(0, (NF - 2) // 4) as it:
                for j in range(4):
                    pe.wait_ge(w_split, DOWN0 + 3 + j + 4 * it)
                    pe.wait_ge(a_split, 3 + j + 4 * it)
                    for t in range(4):
                        down_ring(t, j, last_k=j == 3).then_inc(down_tok, 1)
            down_start(NF, [(k, t) for k in range(2) for t in range(4)],
                       lambda t: pe.wait_ge(ff_dve if t % 2 else ff_act, t // 2 + 1))
            with pe.Fori(0, 4) as it:
                for j in range(4):
                    pe.wait_ge(w_split, DOWN0 + NF + 3 + j + 4 * it)
                    pe.wait_ge(a_split, NF + 3 + j + 4 * it)
                    for t in range(4):
                        down_ring(t, j).then_inc(down_tok, 1)
            for t in range(4):
                tok = slice(t * P, (t + 1) * P)
                for c in range(2):
                    cols = slice(c * HALF, (c + 1) * HALF)
                    for j in range(TAIL):
                        if t == 0 and c == 0:
                            pe.wait_ge(w_split, DOWN0 + 2 * NF - TAIL + j + 1)
                            pe.wait_ge(a_split, 2 * NF - TAIL + j + 1)
                        last = product(ps[:, 2 * t + c, :], a_tail_hi[:, j, tok],
                                       a_tail_lo[:, j, tok], w_tail_hi[:, j, cols],
                                       w_tail_lo[:, j, cols], False, j == TAIL - 1, True)
                    last.then_inc(tail_done, 1)


_INS = ["x", "norm_mix_pre", "w_in", "pool_w", "pool_scale", "conv_w", "attn_sinks", "w_o",
        "norm_mix_post", "norm_ffn_pre", "ffn_w_up", "ffn_conv_w", "ffn_conv_b", "ffn_w_down",
        "norm_ffn_post"]


def shape_constants():
    at = np.arange(P)
    count = np.zeros((P, 2, PAD), np.float32)
    window = np.zeros((P, 2), np.float32)
    for g, w in enumerate(POOL_WINDOWS):
        rows = slice(HD * (g % 2), HD * (g % 2 + 1))
        count[rows, g // 2] = 1.0 / np.minimum(np.arange(1, PAD + 1), w)
        window[rows, g // 2] = 1.0 / w
    return np.ascontiguousarray(np.concatenate(
        [np.eye(P), at[None, :] > at[:, None], at[None, :] >= at[:, None],
         at[None, :] < at[:, None], count.reshape(P, -1), window], axis=1).astype(np.float32))


def kernel(**inputs):
    import concourse.bacc as bacc
    from concourse.bass_utils import run_bass_kernel_spmd

    nc = bacc.Bacc("TRN2", target_bir_lowering=False, num_devices=1)
    arrays = {"consts_dram": shape_constants()}
    arrays.update({f"in_{name}": np.ascontiguousarray(inputs[name]) for name in _INS})
    args = [nc.dram_tensor(name, a.shape, F32, kind="ExternalInput").ap()
            for name, a in arrays.items()]
    out = nc.dram_tensor("out_0", (1, SEQ, DM), F32, kind="ExternalOutput").ap()
    build(nc, *args, out)
    r = run_bass_kernel_spmd(nc, [arrays], core_ids=[0])
    return r.results[0]["out_0"]
```
